# Optimizing a Trainium2 kernel written in Bass

```python
import jax, jax.numpy as jnp
from jax import lax
import numpy as np

D_MODEL = 2048
BATCH = 1
SEQ = 128
DEPTH = 1
DEC_BATCH = 1
DEC_SEQ = 512
PAST_LEN = 128

GRID_W = 64
A_HEADS = 16
A_KV_HEADS = 4
A_GROUP = A_HEADS // A_KV_HEADS
A_HEAD_DIM = 64
A_WIDTH = A_HEADS * A_HEAD_DIM
A_KV_WIDTH = A_KV_HEADS * A_HEAD_DIM
WINDOW = 128
BLOCK = 128
ROPE_BASE = 10000.0
M_HEADS = 4
M_HEAD_DIM = 256
M_WIDTH = M_HEADS * M_HEAD_DIM
M_CHUNK = 64
EPS = 1e-6
NEG_INF = -1e30
SPLITS = (A_WIDTH, A_KV_WIDTH, A_KV_WIDTH, A_WIDTH,
          M_WIDTH, M_WIDTH, M_WIDTH, M_WIDTH, M_WIDTH, 4 * M_HEADS,
          D_MODEL, D_MODEL)
IN_WIDTH = sum(SPLITS)

kernel_name = 'hybrid_mlstm_swa_diffusion_step'

def rmsnorm(x, w):
    xf = x.astype(jnp.float32)
    y = xf * lax.rsqrt(jnp.mean(xf * xf, axis=-1, keepdims=True) + EPS)
    return (y * w.astype(jnp.float32)).astype(x.dtype)

def modulation(cvec, w_ada, b_ada):
    mod = jax.nn.silu(cvec) @ w_ada + b_ada
    shift, scale, gate = jnp.split(mod[:, None, :], 3, axis=-1)
    return shift, scale, gate

def split_proj(u, w_in):
    cuts = np.cumsum(SPLITS)[:-1].tolist()
    return jnp.split(u @ w_in, cuts, axis=-1)

def axial_rope(x):
    T = x.shape[1]
    n_rows = T // GRID_W
    rows = jnp.repeat(jnp.arange(n_rows, dtype=jnp.float32), GRID_W)
    cols = jnp.tile(jnp.arange(GRID_W, dtype=jnp.float32), n_rows)
    half = A_HEAD_DIM // 2
    nf = half // 2
    inv_freq = ROPE_BASE ** (-jnp.arange(nf, dtype=jnp.float32) / nf)
    bshape = (1, T) + (1,) * (x.ndim - 3) + (nf,)

    def rotate(xh, pos):
        ang = (pos[:, None] * inv_freq[None, :]).reshape(bshape)
        cos, sin = jnp.cos(ang), jnp.sin(ang)
        x1, x2 = xh[..., :nf], xh[..., nf:]
        return jnp.concatenate([x1 * cos - x2 * sin, x1 * sin + x2 * cos], axis=-1)

    xf = x.astype(jnp.float32)
    out = jnp.concatenate([rotate(xf[..., :half], rows), rotate(xf[..., half:], cols)], axis=-1)
    return out.astype(x.dtype)

def sink_softmax(s, sink):
    m = jnp.maximum(jnp.max(s, axis=-1, keepdims=True), sink)
    p = jnp.exp(s - m)
    return p / (jnp.sum(p, axis=-1, keepdims=True) + jnp.exp(sink - m))

def context_attention(q, k, v, sink):
    B, S = q.shape[:2]
    s = jnp.einsum('bqkgd,bskd->bkgqs', q, k).astype(jnp.float32) * (A_HEAD_DIM ** -0.5)
    sk = sink.astype(jnp.float32).reshape(1, A_KV_HEADS, A_GROUP, 1, 1)
    p = sink_softmax(s, sk).astype(v.dtype)
    o = jnp.einsum('bkgqs,bskd->bqkgd', p, v)
    return o.reshape(B, S, A_WIDTH)

def latent_attention(q, k, v, ck, cv, sink):
    B, T = q.shape[:2]
    nb = T // BLOCK
    scale = A_HEAD_DIM ** -0.5
    qb = q.reshape(B, nb, BLOCK, A_KV_HEADS, A_GROUP, A_HEAD_DIM)
    pad = ((0, 0), (BLOCK, BLOCK), (0, 0), (0, 0))

    def band(a):
        ap = jnp.pad(a, pad).reshape(B, nb + 2, BLOCK, A_KV_HEADS, A_HEAD_DIM)
        return jnp.concatenate([ap[:, :-2], ap[:, 1:-1], ap[:, 2:]], axis=2)

    kb, vb = band(k), band(v)
    qpos = jnp.arange(nb)[:, None] * BLOCK + jnp.arange(BLOCK)[None, :]
    kpos = (jnp.arange(nb)[:, None] - 1) * BLOCK + jnp.arange(3 * BLOCK)[None, :]
    kp = kpos[:, None, :]
    allowed = (jnp.abs(kp - qpos[:, :, None]) <= WINDOW) & (kp >= 0) & (kp < T)
    s_loc = jnp.einsum('bnqkgd,bnskd->bnkgqs', qb, kb).astype(jnp.float32) * scale
    s_loc = jnp.where(allowed[None, :, None, None], s_loc, NEG_INF)
    s_ctx = jnp.einsum('bnqkgd,bpkd->bnkgqp', qb, ck).astype(jnp.float32) * scale
    s = jnp.concatenate([s_loc, s_ctx], axis=-1)
    sk = sink.astype(jnp.float32).reshape(1, 1, A_KV_HEADS, A_GROUP, 1, 1)
    p = sink_softmax(s, sk).astype(v.dtype)
    nloc = 3 * BLOCK
    o = (jnp.einsum('bnkgqs,bnskd->bnqkgd', p[..., :nloc], vb)
         + jnp.einsum('bnkgqp,bpkd->bnqkgd', p[..., nloc:], cv))
    return o.reshape(B, T, A_WIDTH)

def mlstm_scan(q, k, v, log_i, log_f, C0, n0, m0):
    B, T, H, D = q.shape
    L = M_CHUNK
    nc = T // L

    def to_chunks(a):
        return jnp.moveaxis(a.reshape((B, nc, L) + a.shape[2:]), 1, 0)

    xs = tuple(to_chunks(a) for a in (q, k, v, log_i, log_f))
    tri = jnp.tril(jnp.ones((L, L), dtype=bool))

    def step(carry, inp):
        C, n, m = carry
        qc, kc, vc, ic, fc = inp
        b = jnp.cumsum(fc, axis=1)
        logD = b[:, :, None, :] - b[:, None, :, :] + ic[:, None, :, :]
        logD = jnp.where(tri[None, :, :, None], logD, -jnp.inf)
        inter = b + m[:, None, :]
        mt = jnp.maximum(inter, jnp.max(logD, axis=2))
        Dm = jnp.exp(logD - mt[:, :, None, :])
        sc = jnp.einsum('bthd,bshd->btsh', qc, kc) * Dm
        w_inter = jnp.exp(inter - mt)
        num = (jnp.einsum('btsh,bshd->bthd', sc, vc)
               + w_inter[..., None] * jnp.einsum('bthk,bhkv->bthv', qc, C))
        den = jnp.sum(sc, axis=2) + w_inter * jnp.einsum('bthk,bhk->bth', qc, n)
        h = num / jnp.maximum(jnp.abs(den), jnp.exp(-mt))[..., None]
        bL = b[:, -1, :]
        logw = bL[:, None, :] - b + ic
        m_new = jnp.maximum(bL + m, jnp.max(logw, axis=1))
        w = jnp.exp(logw - m_new[:, None, :])
        decay = jnp.exp(bL + m - m_new)
        C_new = decay[..., None, None] * C + jnp.einsum('bsh,bshk,bshv->bhkv', w, kc, vc)
        n_new = decay[..., None] * n + jnp.einsum('bsh,bshk->bhk', w, kc)
        return (C_new, n_new, m_new), h

    (C, n, m), hs = lax.scan(step, (C0, n0, m0), xs)
    h = jnp.moveaxis(hs, 0, 1).reshape(B, T, H, D)
    return h, C, n, m

def head_norm(h, w):
    B, T = h.shape[:2]
    mu = jnp.mean(h, axis=-1, keepdims=True)
    var = jnp.mean(jnp.square(h - mu), axis=-1, keepdims=True)
    y = (h - mu) * lax.rsqrt(var + EPS)
    return y.reshape(B, T, M_WIDTH) * w.astype(jnp.float32)

def mlstm_branch(mq, mk, mv, mo, mz, mg, b_gates, norm_w, C0, n0, m0):
    B, T = mq.shape[:2]

    def heads(a):
        return a.reshape(B, T, M_HEADS, M_HEAD_DIM).astype(jnp.float32)

    q, k, v = heads(mq), heads(mk) * (M_HEAD_DIM ** -0.5), heads(mv)
    g = mg.astype(jnp.float32) + b_gates.astype(jnp.float32)
    i_f, f_f, i_b, f_b = jnp.split(g, 4, axis=-1)
    C0, n0, m0 = C0.astype(jnp.float32), n0.astype(jnp.float32), m0.astype(jnp.float32)
    h_f, C_f, n_f, m_f = mlstm_scan(q, k, v, i_f, jax.nn.log_sigmoid(f_f), C0[:, 0], n0[:, 0], m0[:, 0])

    def fl(a):
        return jnp.flip(a, axis=1)

    h_b, C_b, n_b, m_b = mlstm_scan(fl(q), fl(k), fl(v), fl(i_b), fl(jax.nn.log_sigmoid(f_b)),
                                    C0[:, 1], n0[:, 1], m0[:, 1])
    h = head_norm(h_f + fl(h_b), norm_w).astype(mq.dtype)
    y = h * jax.nn.sigmoid(mo) * jax.nn.silu(mz)
    C = jnp.stack([C_f, C_b], axis=1)
    n = jnp.stack([n_f, n_b], axis=1)
    m = jnp.stack([m_f, m_b], axis=1)
    return y, C, n, m

def mixer_layer(x, shift, scale, gate, w_in, b_gates, mlstm_norm_w, attn_sink, w_proj_a, w_proj_b,
                w_out, norm_pre_w, norm_post_w, C0, n0, m0, ctx_kv):
    B, T = x.shape[:2]
    u = rmsnorm(x, norm_pre_w) * (1 + scale) + shift
    aq, ak, av, az, mq, mk, mv, mo, mz, mg, ga, gb = split_proj(u, w_in)
    q = aq.reshape(B, T, A_KV_HEADS, A_GROUP, A_HEAD_DIM)
    k = ak.reshape(B, T, A_KV_HEADS, A_HEAD_DIM)
    v = av.reshape(B, T, A_KV_HEADS, A_HEAD_DIM)
    if ctx_kv is None:
        att = context_attention(q, k, v, attn_sink)
    else:
        att = latent_attention(axial_rope(q), axial_rope(k), v, ctx_kv[0], ctx_kv[1], attn_sink)
    y_b = att * jax.nn.silu(az)
    y_a, C, n, m = mlstm_branch(mq, mk, mv, mo, mz, mg, b_gates, mlstm_norm_w, C0, n0, m0)
    merged = jax.nn.sigmoid(ga) * (y_a @ w_proj_a) + jax.nn.sigmoid(gb) * (y_b @ w_proj_b)
    out = rmsnorm(merged @ w_out, norm_post_w)
    return x + gate * out, (k, v, C, n, m)

def setup_inputs(seed: int = 0) -> dict:
    key = jax.random.key(seed)
    ks = jax.random.split(key, 20)
    f32 = jnp.float32

    def nrm(k, shape, scale=1.0):
        return jax.random.normal(k, shape, f32) * scale

    H = M_HEADS
    forget_bias = jnp.linspace(3.0, 6.0, H, dtype=f32)
    zeros_h = jnp.zeros((H,), f32)
    b_gates = nrm(ks[13], (DEPTH, 4 * H), 0.01) + jnp.concatenate([zeros_h, forget_bias, zeros_h, forget_bias])[None, :]
    return {
        'x_prompt': nrm(ks[0], (BATCH, SEQ, D_MODEL)),
        'x_sample': nrm(ks[1], (DEC_BATCH, DEC_SEQ, D_MODEL)),
        'cache_k': nrm(ks[2], (DEC_BATCH, DEPTH, PAST_LEN, A_KV_HEADS, A_HEAD_DIM)),
        'cache_v': nrm(ks[3], (DEC_BATCH, DEPTH, PAST_LEN, A_KV_HEADS, A_HEAD_DIM)),
        'state_C': nrm(ks[4], (DEC_BATCH, DEPTH, 2, M_HEADS, M_HEAD_DIM, M_HEAD_DIM), 0.1),
        'state_n': nrm(ks[5], (DEC_BATCH, DEPTH, 2, M_HEADS, M_HEAD_DIM), 0.1),
        'state_m': nrm(ks[6], (DEC_BATCH, DEPTH, 2, M_HEADS)),
        'c': nrm(ks[7], (DEC_BATCH, D_MODEL)),
        'c_ctx': nrm(ks[8], (D_MODEL,)),
        'w_ada': nrm(ks[9], (DEPTH, D_MODEL, 3 * D_MODEL), 0.5 * D_MODEL ** -0.5),
        'b_ada': nrm(ks[10], (DEPTH, 3 * D_MODEL), 0.02),
        'norm_pre_w': 1.0 + nrm(ks[11], (DEPTH, D_MODEL), 0.02),
        'norm_post_w': 1.0 + nrm(ks[12], (DEPTH, D_MODEL), 0.02),
        'w_in': nrm(ks[14], (DEPTH, D_MODEL, IN_WIDTH), D_MODEL ** -0.5),
        'b_gates': b_gates,
        'mlstm_norm_w': 1.0 + nrm(ks[15], (DEPTH, M_WIDTH), 0.02),
        'attn_sink': nrm(ks[16], (DEPTH, A_HEADS), 0.5),
        'w_proj_a': nrm(ks[17], (DEPTH, M_WIDTH, D_MODEL), M_WIDTH ** -0.5),
        'w_proj_b': nrm(ks[18], (DEPTH, A_WIDTH, D_MODEL), A_WIDTH ** -0.5),
        'w_out': nrm(ks[19], (DEPTH, D_MODEL, D_MODEL), D_MODEL ** -0.5),
    }

def reference(x_prompt, x_sample, cache_k, cache_v, state_C, state_n, state_m, c, c_ctx,
              w_ada, b_ada, norm_pre_w, norm_post_w, w_in, b_gates, mlstm_norm_w, attn_sink,
              w_proj_a, w_proj_b, w_out):
    yp, ys = x_prompt, x_sample
    Bp = x_prompt.shape[0]
    out_k, out_v, out_C, out_n, out_m = [], [], [], [], []
    for l in range(DEPTH):
        sh_p, sc_p, gt_p = modulation(c_ctx[None, :], w_ada[l], b_ada[l])
        zC = jnp.zeros((Bp, 2, M_HEADS, M_HEAD_DIM, M_HEAD_DIM), jnp.float32)
        zn = jnp.zeros((Bp, 2, M_HEADS, M_HEAD_DIM), jnp.float32)
        zm = jnp.zeros((Bp, 2, M_HEADS), jnp.float32)
        yp, (k_l, v_l, C_l, n_l, m_l) = mixer_layer(
            yp, sh_p, sc_p, gt_p, w_in[l], b_gates[l], mlstm_norm_w[l], attn_sink[l],
            w_proj_a[l], w_proj_b[l], w_out[l], norm_pre_w[l], norm_post_w[l], zC, zn, zm, None)
        out_k.append(k_l)
        out_v.append(v_l)
        out_C.append(C_l.astype(x_prompt.dtype))
        out_n.append(n_l.astype(x_prompt.dtype))
        out_m.append(m_l.astype(x_prompt.dtype))
        sh_s, sc_s, gt_s = modulation(c, w_ada[l], b_ada[l])
        ys, _ = mixer_layer(
            ys, sh_s, sc_s, gt_s, w_in[l], b_gates[l], mlstm_norm_w[l], attn_sink[l],
            w_proj_a[l], w_proj_b[l], w_out[l], norm_pre_w[l], norm_post_w[l],
            state_C[:, l], state_n[:, l], state_m[:, l], (cache_k[:, l], cache_v[:, l]))
    return (yp, ys, jnp.stack(out_k, axis=1), jnp.stack(out_v, axis=1), jnp.stack(out_C, axis=1),
            jnp.stack(out_n, axis=1), jnp.stack(out_m, axis=1))


_drawn_inputs = setup_inputs


def setup_inputs(seed=0):
    import zlib

    import numpy as np

    out = dict(_drawn_inputs(seed))
    spreads = {}
    factors = {'state_n': 4.036,
     'state_m': 2.704,
     'norm_post_w': 24.817,
     'mlstm_norm_w': 24.791,
     'attn_sink': 33.924,
     'cache_k': 5.813,
     'cache_v': 4.86}
    for name, (base, spread) in spreads.items():
        noise = np.random.default_rng([zlib.crc32(name.encode()), seed]).standard_normal(out[name].shape)
        drawn = base * np.exp(spread * noise) if base else spread * noise
        out[name] = __import__('jax').numpy.asarray(drawn.astype(out[name].dtype))
    for name, factor in factors.items():
        out[name] = (out[name] * factor).astype(out[name].dtype)
    return out
```

```python
from contextlib import ExitStack

import numpy as np

import concourse.bass as bass
from concourse import mybir

F32 = mybir.dt.float32
F32R = mybir.dt.float32r
ALU = mybir.AluOpType
ACT = mybir.ActivationFunctionType
AX_X = mybir.AxisListType.X

P = 128
D = 2048
KT = D // P
LAT, CTX = 512, 128
TOK = LAT + CTX
HALF_TOK = TOK // 2
NB = LAT // P
A_HEADS, KV_HEADS, HD = 16, 4, 64
M_HEADS, MD = 4, 256
EPS = 1e-6
NEG = -1e30
SCALE = HD ** -0.5
KSCALE = MD ** -0.5

COL_M = 2560
COL_SCAN = 7680
COL_MERGE = 7696
RB_K, RB_V, RB_Z = 8, 10, 12
RB_MQ, RB_MK, RB_MV, RB_MO, RB_MZ = 20, 28, 36, 44, 52
RB_SCAN, RB_GA, RB_GB = 60, 61, 77
RB_ALL = 93

T_L0, T_L1, T_L2, T_MERGE, T_OUT, T_END = 5, 21, 69, 93, 109, 125
L1_TILES, L2_TILES = 12, 6
ADA_USES = 16

C_IDENT, C_TRIF, C_TRIB, C_PERM, C_BAND, C_COS, C_SIN, C_END = 0, 128, 256, 384, 512, 2048, 2560, 3072


def shape_constants():
    t = np.zeros((P, C_END), np.float32)
    row, col = np.arange(P)[:, None], np.arange(P)[None, :]
    t[:, C_IDENT:C_IDENT + P] = row == col
    t[:, C_TRIF:C_TRIF + P] = np.where(row <= col, 0.0, NEG)
    t[:, C_TRIB:C_TRIB + P] = np.where(row >= col, 0.0, NEG)
    t[:, C_PERM:C_PERM + P] = np.where(col % 32 < 16, -1.0 * (row == col + 16), 1.0 * (row == col - 16))
    left, right, full = np.where(col >= row, 0.0, NEG), np.where(col <= row, 0.0, NEG), np.full((P, P), NEG)
    for i, (lo, hi) in enumerate(((full, right), (left, right), (left, full))):
        t[:, C_BAND + 512 * i:C_BAND + 512 * i + P] = lo
        t[:, C_BAND + 512 * i + 256:C_BAND + 512 * i + 384] = hi
    pos = np.arange(LAT)
    freq = np.float32(10000.0) ** (-np.arange(16, dtype=np.float32) / np.float32(16))
    for d in range(P):
        at = (pos // 64 if d % 64 < 32 else pos % 64).astype(np.float32)
        ang = at * freq[d % 16]
        t[d, C_COS:C_COS + LAT] = np.cos(ang)
        t[d, C_SIN:C_SIN + LAT] = np.sin(ang)
    return t


class Chain:

    def __init__(self, eng, sem):
        self.eng, self.sem, self.n, self.i, self.per = eng, sem, 0, 0, 0

    def link(self, ins):
        ins.then_inc(self.sem, 1)
        self.n += 1
        self.eng.wait_ge(self.sem, self.n + self.per * self.i)

    def enter(self, i, per):
        self.start, self.i, self.per = self.n, i, per

    def leave(self, times):
        assert self.n - self.start == self.per, (self.n - self.start, self.per)
        self.n = self.start + self.per * times
        self.i = self.per = 0


def hybrid_layer(nc, x_prompt, x_sample, cache_k, cache_v, state_C, state_n, state_m, c, c_ctx, w_ada, b_ada,
                 norm_pre_w, norm_post_w, w_in, b_gates, mlstm_norm_w, attn_sink, w_proj_a, w_proj_b, w_out,
                 constants, y_prompt, y_sample, new_k, new_v, new_C, new_n, new_m):
    proj = nc.dram_tensor("proj_dram", (RB_ALL * P, TOK), F32, kind="Internal").ap()
    rrow = nc.dram_tensor("rrow_dram", (2 * M_HEADS, TOK), F32, kind="Internal").ap()
    gsum = nc.dram_tensor("gsum_dram", (P, 2 * D), F32, kind="Internal").ap()
    w_in_v = w_in[0].rearrange("(k p) n -> p k n", p=P)
    w_ada_v = w_ada[0].rearrange("(k p) n -> p k n", p=P)
    w_pa_v = w_proj_a[0].rearrange("(k p) n -> p k n", p=P)
    w_pb_v = w_proj_b[0].rearrange("(k p) n -> p k n", p=P)
    w_out_v = w_out[0].rearrange("(k p) n -> p k n", p=P)

    with ExitStack() as ctx:
        def sb(name, shape, dt=F32):
            return ctx.enter_context(nc.sbuf_tensor(name, shape, dt))

        def sem(name):
            return ctx.enter_context(nc.semaphore(name))

        bank = [ctx.enter_context(nc.psum_tensor(f"bank{i}", [P, 512], F32)) for i in range(8)]
        ab = bank[4:8]

        XH = sb("XH", [P, KT, TOK], F32R)
        XL = sb("XL", [P, KT, TOK], F32R)
        Y = sb("Y", [P, KT, TOK])
        RAW = sb("RAW", [P, 4, 1024])
        WH = sb("WH", [P, 2, 1024], F32R)
        WL = sb("WL", [P, 2, 1024], F32R)
        OUTS = sb("OUTS", [P, 2, TOK])
        CK = sb("CK", [P, 384])
        ROWS = sb("ROWS", [88, P])
        VC = sb("VC", [P, 88])
        MODS = sb("MODS", [P, 32, 2])
        SCL = sb("SCL", [P, KT, 2])
        ONES = sb("ONES", [P, P])
        SS = sb("SS", [P, 5])
        RSTD = sb("RSTD", [P, 5])
        COLS = sb("COLS", [P, 5, 100])
        COLH = sb("COLH", [P, 5, 4])
        M0B = sb("M0B", [P, 2, M_HEADS])
        M0H = sb("M0H", [P, 2])
        MNH = sb("MNH", [P, 2])
        ENM = sb("ENM", [P, 5, 2])
        DEN = sb("DEN", [P, 2])
        ZERO = sb("ZERO", [P, 8])
        HP = sb("HP", [P, 1])
        WORK = sb("WORK", [P, 11500])

        ident = CK[:, 0:P]
        tri = [CK[:, P:2 * P], CK[:, 2 * P:3 * P]]
        cursor = [0]

        def work(n, shape=None, **kw):
            at = cursor[0]
            cursor[0] += n
            assert cursor[0] <= 11500, cursor[0]
            v = WORK[:, at:at + n]
            return v.rearrange(shape, **kw) if shape else v

        GI, GF, GT, GB, GM = (work(TOK) for _ in range(5))
        BIAS = work(2)
        M0R = work(1)
        TA = work(TOK)
        AR = work(2048, "p (s n) -> p s n", s=2)
        SQ = AR.rearrange("p s n -> p (s n)")
        MR = work(1024, "p (u n) -> p u n", u=2)
        cursor[0] = 11500 - 2 * D
        GACC = work(2 * D, "p (v n) -> p v n", v=2)
        cursor[0] = 0
        AC = work(C_END - C_PERM)
        perm = AC[:, 0:P]
        band = [AC[:, C_BAND - C_PERM + 512 * i:C_BAND - C_PERM + 512 * (i + 1)] for i in range(3)]
        cos, sin = AC[:, C_COS - C_PERM:C_SIN - C_PERM], AC[:, C_SIN - C_PERM:C_END - C_PERM]
        QT = work(2 * TOK, "p (c t) -> p c t", c=2)
        ZT = work(2 * TOK, "p (c t) -> p c t", c=2)
        KK = work(1024)
        VVT = work(TOK)
        VA = work(6 * HD, "p (b d) -> p b d", b=6)
        CKG = work(2 * HD)
        KO = work(HD)
        SINK = work(4)
        PR = work(2 * 2 * 512, "p (u e s) -> p u e s", u=2, e=2)
        EZ = PR.rearrange("p u e s -> p (u e s)")[:, 0:2 * TOK]
        PT = work(2 * 512, "p (e s) -> p e s", e=2)
        OB = work(2 * HD)
        RT = work(512)
        MX = work(8)
        NM, SE, RSUM, RDEN = MX[:, 0:2], MX[:, 2:4], MX[:, 4:6], MX[:, 6:8]
        MXR = work(2)
        attention_end = cursor[0]
        cursor[0] = 0
        MQ = work(2 * TOK, "p (c t) -> p c t", c=2)
        mk_at = cursor[0]
        MK = work(2 * TOK, "p (c t) -> p c t", c=2)
        mv_at = cursor[0]
        MVT = work(2 * TOK, "p (c t) -> p c t", c=2)
        QSF = WORK[:, mk_at:mk_at + 2 * LAT].rearrange("p (c t) -> p c t", c=2)
        PF = WORK[:, mv_at:mv_at + 1280]
        VT = work(5 * 257, "p (b d) -> p b d", b=5)
        KP = work(MD)
        KW = work(2 * MD, "p (r d) -> p r d", r=2)
        CA = work(2 * 2 * 257, "p (r c d) -> p r c d", r=2, c=2)
        RB = work(2 * TOK, "p (r t) -> p r t", r=2)
        HH = RB.rearrange("p r t -> p (r t)").rearrange("p (b d) -> p b d", b=5)
        QSB = work(2 * LAT, "p (c t) -> p c t", c=2)
        PB = work(1280)
        PP = work(2 * P, "p (r t) -> p r t", r=2)
        BNS = work(30, "p (b s) -> p b s", b=5)
        MVAR = work(10, "p (b s) -> p b s", b=5)
        MRS = work(5)
        QS, PM = [QSF, QSB], [PF, PB]
        cursor[0] = 0
        GAB = work(2 * 2 * TOK, "p (u g t) -> p u g t", u=2, g=2)
        MT = work(2 * TOK, "p (g t) -> p g t", g=2)
        cursor[0] = 0
        GW = work(2 * D, "p (g n) -> p g n", g=2)
        xr_at = cursor[0]
        XR = work(3 * D, "p (u n) -> p u n", u=3)
        GS = WORK[:, xr_at:xr_at + 2 * D].rearrange("p (v n) -> p v n", v=2)
        NPW = WORK[:, xr_at + 2 * D:xr_at + 3 * D]
        SSQ = work(20, "p (b n) -> p b n", b=5)
        SQS = work(512)
        OR = Y[:, :, :].rearrange("p k t -> p (k t)").rearrange("p (b n) -> p b n", b=5)
        XT = OR

        rows_in, const_in, x_in, aconst_in = sem("rows_in"), sem("const_in"), sem("x_in"), sem("aconst_in")
        m0_in, mnull = sem("m0_in"), sem("mnull")
        raw_in = [sem(f"raw_in{i}") for i in range(4)]
        gada_in = [sem(f"gada_in{i}") for i in range(2)]
        mr_zero = sem("mr_zero")
        silu_e, silu_done, rows_t, vc_done = sem("silu_e"), sem("silu_done"), sem("rows_t"), sem("vc_done")
        ada_used, ada_row, ada_t, ada_out = sem("ada_used"), sem("ada_row"), sem("ada_t"), sem("ada_out")
        gada_used, gacc_init, gacc_stored = sem("gada_used"), sem("gacc_init"), sem("gacc_stored")
        gacc_zero, gs_in, ones_set = sem("gacc_zero"), sem("gs_in"), sem("ones_set")
        sq_done, ms_done, rstd_done, xn_done = sem("sq_done"), sem("ms_done"), sem("rstd_done"), sem("xn_done")
        scl_done, xt_psum, u_done, u_hi, u_lo = sem("scl_done"), sem("xt_psum"), sem("u_done"), sem("u_hi"), sem("u_lo")
        hi_done, lo_done, w_used = sem("hi_done"), sem("lo_done"), sem("w_used")
        out_ready = sem("out_ready")
        spilled = [sem(f"spilled{i}") for i in range(2)]
        scan_zero, scan_in, scan_t, scan_e, scan_ln, scan_rows, scan_stored = (
            sem(n) for n in ("scan_zero", "scan_in", "scan_t", "scan_e", "scan_ln", "scan_rows", "scan_stored"))
        cols_psum, cols_done = sem("cols_psum"), sem("cols_done")
        pads_zero, att_in, prep_psum, roped, kv_out, kvo_ready, ez_done = (
            sem(n) for n in ("pads_zero", "att_in", "prep_psum", "roped", "kv_out", "kvo_ready", "ez_done"))
        s_psum, neg_max, probs, probs_t, probs_t_sb, o_psum, o_ready, ot_psum, yb_done = (
            sem(n) for n in ("s_psum", "neg_max", "probs", "probs_t", "probs_t_sb", "o_psum", "o_ready", "ot_psum",
                             "yb_done"))
        ones_col, ml_in, ml_gates_in, ml_vt, ml_vt_sb, ml_s, ml_pre, ml_decay, ml_p, ml_sp, ml_pp, ml_w, ml_qs, ml_kw = (
            sem(n) for n in ("ones_col", "ml_in", "ml_gates_in", "ml_vt", "ml_vt_sb", "ml_s", "ml_pre", "ml_decay", "ml_p",
                             "ml_sp", "ml_pp", "ml_w", "ml_qs", "ml_kw"))
        ml_uf, ml_ufd, ml_ub, ml_ubd, ml_up, ml_upd, ml_cb, ml_cbd, ml_state_out = (
            sem(n) for n in ("ml_uf", "ml_ufd", "ml_ub", "ml_ubd", "ml_up", "ml_upd", "ml_cb", "ml_cbd", "ml_state_out"))
        ml_var, ml_rs, ml_h, ml_ht, ml_eg, ml_ya = (
            sem(n) for n in ("ml_var", "ml_rs", "ml_h", "ml_ht", "ml_eg", "ml_ya"))
        y_hi, y_lo, sig_in = sem("y_hi"), sem("y_lo"), [sem("sig_in0"), sem("sig_in1")]
        sig_done, merged = sem("sig_done"), sem("merged")
        m_hi, m_lo, gw_psum, gw_done = sem("m_hi"), sem("m_lo"), sem("gw_psum"), sem("gw_done")
        o_copied, o_sq, o_ms, o_root, o_y, stored = (
            sem(n) for n in ("o_copied", "o_sq", "o_ms", "o_root", "o_y", "stored"))
        xr_in = [sem(f"xr_in{i}") for i in range(3)]
        dve_chain, pool_chain = sem("dve_chain"), sem("pool_chain")

        block = ctx.enter_context(nc.Block())

        @block.sync
        def _(sp):
            sp.dma_start(CK[:, :], constants[:, 0:C_PERM]).then_inc(const_in, 16)
            for r0, src, n in ((0, c[0], 16), (16, c_ctx, 16), (32, norm_pre_w[0], 16), (48, b_ada[0, 0:4096], 32),
                               (80, mlstm_norm_w[0], 8)):
                sp.dma_start(ROWS[r0:r0 + n, :], src.rearrange("(r p) -> r p", p=P)).then_inc(rows_in, 16)

            def ada_chunk(ch):
                for q in range(8):
                    if not (isinstance(ch, int) and q < 4):
                        sp.wait_ge(ada_used, 8 * ch + (q - 3))
                    sp.dma_start(RAW[:, q % 4, :].rearrange("p (k n) -> p k n", k=2),
                                 w_ada_v[:, 2 * q:2 * q + 2, bass.ds(512 * ch, 512)]).then_inc(raw_in[q % 4], 16)

            ada_chunk(0)
            for b in range(5):
                src = x_sample[0, b * P:(b + 1) * P, :] if b < NB else x_prompt[0]
                sp.dma_start(XT[:, b, :], src).then_inc(x_in, 16)
            with sp.Fori(1, 8) as ch:
                ada_chunk(ch)

            def w_half(g_base, g, slot, src, k=8):
                if g_base is not None:
                    sp.wait_ge(lo_done, g_base)
                sp.dma_start(RAW[:, slot, :].rearrange("p (k n) -> p k n", k=k), src).then_inc(raw_in[slot], 16)

            def in_tile(t, i, col):
                for x in range(2):
                    g = 2 * t + x
                    slot = g % 4
                    if isinstance(i, int) and g + i < 4:
                        sp.wait_ge(ada_used, 64 + g - 3)
                        lo = None
                    else:
                        lo = 2 * i + (g - 3)
                    w_half(lo, g, slot, w_in_v[:, 8 * x:8 * x + 8, bass.ds(col, P)])

            in_tile(0, 0, COL_SCAN)
            for t in range(1, T_L0):
                in_tile(t, 0, P * (t - 1))

            def gada_half(ch, q):
                if not (isinstance(ch, int) and q < 2):
                    sp.wait_ge(gada_used, 8 * ch + (q - 1))
                sp.dma_start(AR[:, q % 2, :].rearrange("p (k n) -> p k n", k=2),
                             w_ada_v[:, 2 * q:2 * q + 2, bass.ds(512 * ch + 4096, 512)]).then_inc(gada_in[q % 2], 16)

            def l0_body(ch):
                for k in range(4):
                    in_tile(T_L0 + k, 4 * ch, 512 * ch + P * (T_L0 - 1 + k))
                    gada_half(ch, 2 * k)
                    gada_half(ch, 2 * k + 1)

            sp.wait_ge(sq_done, 5)
            l0_body(0)
            sp.wait_ge(scan_stored, 16 * 4)
            sp.wait_ge(cols_done, 1)
            sp.dma_start(AC, constants[:, C_PERM:C_END]).then_inc(aconst_in, 16)
            with sp.Fori(1, 4) as ch:
                l0_body(ch)
            sp.wait_ge(gada_used, 32)
            sp.dma_start(gsum, GACC.rearrange("p v n -> p (v n)")).then_inc(gacc_stored, 16)
            with sp.Fori(0, 4) as g:
                for k in range(L1_TILES):
                    col = COL_MERGE + P * k + 2 * P * g if k < 2 else COL_M + P * (k - 2) + 10 * P * g
                    in_tile(T_L1 + k, L1_TILES * g, col)
                    if k == 4:
                        sp.wait_ge(kvo_ready, g + 1)
                        sp.dma_start(new_k[0, 0, :, g, :], KO).then_inc(kv_out, 16)
                        sp.dma_start(new_v[0, 0, :, g, :], VA[:, NB, :]).then_inc(kv_out, 16)
            with sp.Fori(0, 4) as h:
                def states_out(r):
                    for cc in range(2):
                        sp.dma_start(new_C[0, 0, r, h, cc * P:(cc + 1) * P, :], CA[:, r, cc, 0:MD])\
                            .then_inc(ml_state_out, 16)
                        sp.dma_start(new_n[0, 0, r, h, cc * P:(cc + 1) * P].rearrange("(p o) -> p o", o=1),
                                       CA[:, r, cc, MD:MD + 1]).then_inc(ml_state_out, 16)

                for k in range(L2_TILES):
                    in_tile(T_L2 + k, L2_TILES * h, COL_MERGE + P * (8 + k) + L2_TILES * P * h)
                sp.wait_ge(ml_upd, h + 1)
                states_out(0)
                sp.wait_ge(ml_cbd, h + 1)
                states_out(1)
            with sp.Fori(0, 8) as i:
                for k in range(2):
                    for x, wv in ((0, w_pa_v), (1, w_pb_v)):
                        g = 2 * (T_MERGE + k) + x
                        w_half(4 * i + (g - 3), g, g % 4, wv[:, :, bass.ds(P * k + 2 * P * i, P)])
            with sp.Fori(0, 4) as n:
                for q in range(8):
                    g = 2 * T_OUT + q
                    w_half(8 * n + (g - 3), g, g % 4, w_out_v[:, 2 * q:2 * q + 2, bass.ds(512 * n, 512)], k=2)
            sp.wait_ge(stored, 16 * 5)
            sp.wait_ge(kv_out, 16 * 8 + 16)
            sp.wait_ge(ml_state_out, 16 * 8 * M_HEADS + 16)

        @block.gpsimd
        def _(pool):
            chain = Chain(pool, pool_chain)

            nc.gpsimd.memset(HP[:, :], -0.5).then_inc(mnull, 1)
            for n, (s, used) in enumerate(((yb_done, 1), (kv_out, 16), (ml_ya, 1), (ml_state_out, 16),
                                           (merged, 1), (o_sq, 1))):
                nc.gpsimd.memset(ZERO[:, n:n + 1], 0.0).then_inc(s, used)
            nc.gpsimd.memset(MR, 0.0).then_inc(mr_zero, 1)
            pool.dma_start(M0B[:, :, :].rearrange("p r h -> p (r h)"),
                           state_m[0, 0].rearrange("r h -> (r h)").partition_broadcast(P)).then_inc(m0_in, 16)

            def spill(t, i, row):
                pool.wait_ge(out_ready, i + (t + 1))
                pool.dma_start(proj[bass.ds(row * P, P), :], OUTS[:, t % 2, :]).then_inc(spilled[t % 2], 16)

            nc.gpsimd.memset(ONES[:, :], 1.0).then_inc(ones_set, 1)
            nc.gpsimd.memset(GACC, 0.0).then_inc(gacc_zero, 1)
            pool.wait_ge(gacc_zero, 1)
            for v in range(2):
                pool.dma_start(GACC[0:1, v, :], b_ada[0:1, 4096:6144]).then_inc(gacc_init, 16)
            for a in (GI, GF, TA):
                chain.link(nc.gpsimd.memset(a[0:100, :], 0.0))
            chain.link(nc.gpsimd.memset(BIAS[0:36, :], 0.0))
            chain.link(nc.gpsimd.memset(M0R[0:36, :], 0.0))
            for r, tile, col in ((0, GI, 0), (4, GF, 1), (8, GI, 0), (12, GF, 1)):
                at = 32 * (r // 8)
                pool.dma_start(BIAS[at:at + 4, col:col + 1],
                               b_gates[0, r:r + 4].rearrange("(p o) -> p o", o=1)).then_inc(scan_in, 16)
            for r in range(2):
                pool.dma_start(M0R[32 * r:32 * r + 4, :],
                               state_m[0, 0, r].rearrange("(p o) -> p o", o=1)).then_inc(scan_in, 16)
            pool.wait_ge(mnull, 1)
            pool.wait_ge(ms_done, 1)
            nc.gpsimd.tensor_tensor(RSTD[:, :], SS[:, :], HP[:, 0:1].to_broadcast([P, 5]), ALU.pow).then_inc(rstd_done, 1)
            spill(0, 0, RB_SCAN)
            pool.wait_ge(spilled[0], 16)
            for r, tile in ((0, GI), (4, GF), (8, GI), (12, GF)):
                at = 32 * (r // 8)
                pool.dma_start(tile[at:at + 4, :], proj[RB_SCAN * P + r:RB_SCAN * P + r + 4, :]).then_inc(scan_in, 16)
            for t in range(1, T_L0):
                spill(t, 0, t - 1)
                if t == 2:
                    pool.wait_ge(scan_rows, 1)
                    for r in range(2):
                        at = 32 * r
                        end = TOK - 1 if r == 0 else LAT
                        pool.dma_start(rrow[4 * r:4 * r + 4, :], GF[at:at + 4, :]).then_inc(scan_stored, 16)
                        pool.dma_start(new_m[0, 0, r].rearrange("(p o) -> p o", o=1),
                                       GM[at:at + 4, end:end + 1]).then_inc(scan_stored, 16)
            with pool.Fori(0, 4) as ch:
                for k in range(4):
                    spill(T_L0 + k, 4 * ch, 4 * ch + (T_L0 - 1 + k))

            pool.wait_ge(gacc_stored, 16)
            pool.wait_ge(scan_stored, 16 * 4)
            pool.wait_ge(cols_done, 1)
            chain.link(nc.gpsimd.memset(KK[:, 0:P], 0.0))
            nc.gpsimd.memset(KK[:, P + LAT:2 * P + LAT], 0.0).then_inc(pads_zero, 1)
            pool.wait_ge(spilled[0], 16 * ((T_L1 + 1) // 2))
            pool.wait_ge(spilled[1], 16 * (T_L1 // 2))
            with pool.Fori(0, KV_HEADS) as g:
                pool.wait_ge(yb_done, 10 * g + 1)
                pool.wait_ge(kv_out, 32 * g + 16)
                pool.dma_start(QT, proj[bass.ds(256 * g, 256), :].rearrange("(c p) t -> p c t", p=P)).then_inc(att_in, 16)
                pool.dma_start(ZT, proj[bass.ds(256 * g + RB_Z * P, 256), :].rearrange("(c p) t -> p c t", p=P))\
                    .then_inc(att_in, 16)
                for e in range(2):
                    rows = proj[bass.ds(HD * g + RB_K * P, HD), :]
                    pool.dma_start(KK[HD * e:HD * e + HD, P:P + LAT], rows[:, 0:LAT]).then_inc(att_in, 16)
                    pool.dma_start(KK[HD * e:HD * e + HD, 768:896], rows[:, LAT:TOK]).then_inc(att_in, 16)
                    pool.dma_start(CKG[:, HD * e:HD * e + HD], cache_k[0, 0, :, g, :]).then_inc(att_in, 16)
                pool.dma_start(VVT[0:HD, :], proj[bass.ds(HD * g + RB_V * P, HD), :]).then_inc(att_in, 16)
                pool.dma_start(VA[:, 5, :], cache_v[0, 0, :, g, :]).then_inc(att_in, 16)
                pool.dma_start(SINK, attn_sink[0, bass.ds(4 * g, 4)].partition_broadcast(P)).then_inc(att_in, 16)
                for k in range(L1_TILES):
                    row = RB_GA + k + 2 * g if k < 2 else RB_MQ + (k - 2) + 10 * g
                    spill(T_L1 + k, L1_TILES * g, row)

            pool.wait_ge(yb_done, 10 * KV_HEADS + 1)
            pool.wait_ge(kv_out, 32 * KV_HEADS + 16)
            nc.gpsimd.memset(VT[:, :, MD:MD + 1], 1.0).then_inc(ones_col, 1)
            pool.wait_ge(spilled[0], 16 * ((T_L2 + 1) // 2))
            pool.wait_ge(spilled[1], 16 * (T_L2 // 2))

            def head_rows(rb, h):
                return proj[bass.ds(2 * P * h + rb * P, 2 * P), :].rearrange("(c p) t -> p c t", p=P)

            pool.wait_ge(mnull, 1)
            with pool.Fori(0, M_HEADS) as h:
                pool.wait_ge(ml_ya, h + 1)
                pool.wait_ge(ml_state_out, 128 * h + 16)
                for dst, rb in ((MQ, RB_MQ), (MK, RB_MK), (MVT, RB_MV)):
                    pool.dma_start(dst, head_rows(rb, h)).then_inc(ml_in, 16)
                for r in range(2):
                    pool.dma_start(CA[:, r, :, 0:MD],
                                   state_C[0, 0, r, h, :, :].rearrange("(c p) v -> p c v", p=P)).then_inc(ml_in, 16)
                    for cc in range(2):
                        pool.dma_start(CA[:, r, cc, MD:MD + 1],
                                       state_n[0, 0, r, h, cc * P:(cc + 1) * P].rearrange("(p o) -> p o", o=1))\
                            .then_inc(ml_in, 16)
                    pool.dma_start(RB[:, r, :], rrow[h + 4 * r, :].partition_broadcast(P)).then_inc(ml_in, 16)

                for k in range(L2_TILES):
                    spill(T_L2 + k, L2_TILES * h, RB_GA + 8 + k + L2_TILES * h)
                    if k == 2:
                        pool.wait_ge(ml_ub, h + 1)
                        pool.wait_ge(ml_kw, h + 1)
                        pool.dma_start(MK, head_rows(RB_MO, h)).then_inc(ml_gates_in, 16)
                        pool.dma_start(MVT, head_rows(RB_MZ, h)).then_inc(ml_gates_in, 16)
                    if k == 3:
                        pool.wait_ge(ml_var, h + 1)
                        nc.gpsimd.tensor_tensor(MRS, MVAR[:, :, 1], HP[:, 0:1].to_broadcast([P, 5]),
                                                ALU.pow).then_inc(ml_rs, 1)

            pool.wait_ge(ml_ya, M_HEADS + 1)
            pool.wait_ge(spilled[0], 16 * ((T_MERGE + 1) // 2))
            pool.wait_ge(spilled[1], 16 * (T_MERGE // 2))

            def merge_gates(j, u):
                for gi, rb in ((0, RB_GA), (1, RB_GB)):
                    pool.dma_start(GAB[:, u, gi, :], proj[bass.ds((rb + j) * P, P), :]).then_inc(sig_in[u], 16)

            merge_gates(0, 0)
            merge_gates(1, 1)
            pool.wait_ge(ml_state_out, 128 * M_HEADS + 16)
            pool.dma_start(GS.rearrange("p v n -> p (v n)"), gsum).then_inc(gs_in, 16)
            pool.dma_start(NPW, norm_post_w[0].partition_broadcast(P)).then_inc(gs_in, 16)
            with pool.Fori(1, 8) as i:
                for u in range(2):
                    pool.wait_ge(merged, 2 * i + u)
                    merge_gates(2 * i + u, u)

            pool.wait_ge(gw_done, 8)
            for b in range(5):
                if b == 3:
                    pool.wait_ge(o_ms, 1)
                    nc.gpsimd.tensor_tensor(RSTD[:, :], SS[:, :], HP[:, 0:1].to_broadcast([P, 5]),
                                            ALU.pow).then_inc(o_root, 1)
                if b >= 3:
                    pool.wait_ge(o_y, b - 2)
                src = x_sample[0, b * P:(b + 1) * P, :] if b < NB else x_prompt[0]
                pool.dma_start(XR[:, b % 3, :], src).then_inc(xr_in[b % 3], 16)
                if b == 3:
                    pool.dma_start(y_sample[0, 0:P, :], OR[:, 0, :]).then_inc(stored, 16)
            for b in range(1, 5):
                pool.wait_ge(o_y, b + 1)
                dst = y_sample[0, b * P:(b + 1) * P, :] if b < NB else y_prompt[0]
                pool.dma_start(dst, OR[:, b, :]).then_inc(stored, 16)

        @block.scalar
        def _(act):
            def hi(i, per, gs):
                slot = gs % 4
                act.wait_ge(raw_in[slot], 4 * per * i + 16 * (ADA_USES + gs // 4 + 1))
                if not (isinstance(i, int) and gs < 2):
                    act.wait_ge(w_used, per * i + (gs - 1))
                nc.scalar.activation(WH[:, gs % 2, :], RAW[:, slot, :], ACT.Copy).then_inc(hi_done, 1)

            def evac(i, t):
                act.wait_ge(w_used, 2 * i + (2 * t + 2))
                if not (isinstance(i, int) and t + i < 2):
                    act.wait_ge(spilled[t % 2], 8 * i + 16 * (t // 2))
                for n in range(2):
                    ins = nc.scalar.activation(OUTS[:, t % 2, n * HALF_TOK:(n + 1) * HALF_TOK],
                                               bank[2 * (t % 2) + n][:, 0:HALF_TOK], ACT.Copy)
                ins.then_inc(out_ready, 1)

            act.wait_ge(rows_in, 16 * 5)
            nc.scalar.activation(OUTS[0:32, 0, 0:P], ROWS[0:32, :], ACT.Sigmoid).then_inc(silu_e, 1)
            for b in range(5):
                act.wait_ge(x_in, 16 * 5)
                if b:
                    act.wait_ge(sq_done, b)
                nc.scalar.activation(SQ, XT[:, b, :], ACT.Square, accum_out=SS[:, b:b + 1]).then_inc(sq_done, 1)
            act.wait_ge(scl_done, 1)
            for k in range(KT):
                act.wait_ge(xt_psum, k + 1)
                if k >= 2:
                    act.wait_ge(u_lo, k - 1)
                nc.scalar.activation(OUTS[:, k % 2, 0:LAT], bank[2 * (k % 2)][:, :], ACT.Identity,
                                     bias=MODS[:, k, 0:1], scale=SCL[:, k, 0:1])
                nc.scalar.activation(OUTS[:, k % 2, LAT:TOK], bank[2 * (k % 2) + 1][:, 0:CTX], ACT.Identity,
                                     bias=MODS[:, k, 1:2], scale=SCL[:, k, 1:2]).then_inc(u_done, 1)
                if k == 8:
                    hi(0, 0, 0)
            act.wait_ge(u_lo, KT)

            hi(0, 0, 1)
            for t in range(1, T_L0):
                hi(0, 0, 2 * t)
                evac(0, t - 1)
                hi(0, 0, 2 * t + 1)
                if t == 2:
                    act.wait_ge(scan_t, 1)
                    nc.scalar.activation(GB[0:36, :], GB[0:36, :], ACT.Exp).then_inc(scan_e, 1)
                    act.wait_ge(scan_e, 1)
                    nc.scalar.activation(GB[0:36, :], GB[0:36, :], ACT.Ln, bias=1.0).then_inc(scan_ln, 1)
            with act.Fori(0, 4) as ch:
                for k in range(4):
                    hi(ch, 8, 2 * (T_L0 + k))
                    evac(4 * ch, T_L0 + k - 1)
                    hi(ch, 8, 2 * (T_L0 + k) + 1)

            with act.Fori(0, KV_HEADS) as kv:

                def soft(u):
                    par = u % 2
                    act.wait_ge(neg_max, 10 * kv + (u + 1))
                    cols = 512 if u < 8 else P
                    nc.scalar.activation(SE, SE, ACT.Exp)
                    for e in range(2):
                        ins = nc.scalar.activation(PR[:, par, e, 0:cols], PR[:, par, e, 0:cols], ACT.Exp,
                                                   bias=NM[:, e:e + 1], accum_out=RSUM[:, e:e + 1])
                    ins.then_inc(probs, 1)

                def copy_pt(u):
                    act.wait_ge(probs_t, 10 * kv + (u + 1))
                    if u >= 1:
                        act.wait_ge(o_psum, 10 * kv + u)
                    lo, cols = (P, 512) if u < 2 else (0, 512) if u < 8 else (0, P)
                    for e in range(2):
                        ins = nc.scalar.activation(PT[:, e, lo:cols], ab[2 + e][:, lo:cols], ACT.Copy)
                    ins.then_inc(probs_t_sb, 1)

                for s in range(2 * L1_TILES):
                    t, x = divmod(s, 2)
                    hi(kv, 2 * L1_TILES, 2 * T_L1 + s)
                    if x == 0:
                        evac(L1_TILES * kv, T_L1 + t - 1)
                    if s == 1:
                        act.wait_ge(att_in, 11 * 16 * kv + 11 * 16)
                        act.wait_ge(yb_done, 10 * kv + 1)
                        nc.scalar.activation(EZ, ZT.rearrange("p c t -> p (c t)"), ACT.Exp, scale=-1.0).then_inc(ez_done, 1)
                    if s >= 3 and s % 2 == 1 and (s - 3) // 2 < 10:
                        soft((s - 3) // 2)
                    if s >= 4 and s % 2 == 0:
                        copy_pt((s - 4) // 2)

            with act.Fori(0, M_HEADS) as h:

                def decays():
                    act.wait_ge(ml_pre, h + 1)
                    for r in range(2):
                        for i in range(NB):
                            lo = p_at(r, i, i)
                            off = (p_at(r, i, i + 1), (i + 1) * P, LAT) if r == 0 else (p_at(r, i, 0), 0, i * P)
                            nc.scalar.activation(PM[r][:, lo:lo + P], PM[r][:, lo:lo + P], ACT.Exp, bias=COLH[:, i, r:r + 1])
                            if off[2] > off[1]:
                                nc.scalar.activation(PM[r][:, off[0]:off[0] + off[2] - off[1]], RB[:, r, off[1]:off[2]],
                                                     ACT.Exp, bias=COLH[:, i, r:r + 1])
                        ins = nc.scalar.activation(PP[:, r, :], PP[:, r, :], ACT.Exp, bias=COLH[:, NB, r:r + 1])
                    ins.then_inc(ml_decay, 1)

                def inter():
                    act.wait_ge(ml_decay, h + 1)
                    for r in range(2):
                        nc.scalar.activation(RB[:, r, 0:LAT], RB[:, r, 0:LAT], ACT.Exp, bias=M0H[:, r:r + 1])
                    nc.scalar.activation(ENM[:, :, :], COLH[:, :, 2:4], ACT.Exp).then_inc(ml_w, 1)

                def gates():
                    act.wait_ge(ml_gates_in, 32 * h + 32)
                    nc.scalar.activation(MK, MK, ACT.Exp, scale=-1.0)
                    nc.scalar.activation(MQ, MVT, ACT.Exp, scale=-1.0).then_inc(ml_eg, 1)

                for s in range(2 * L2_TILES):
                    t, x = divmod(s, 2)
                    hi(h, 2 * L2_TILES, 2 * T_L2 + s)
                    if x == 0:
                        evac(L2_TILES * h, T_L2 + t - 1)
                    if s == 2:
                        decays()
                        inter()
                    if s == 9:
                        gates()

            hi(0, 0, 2 * T_MERGE)
            evac(0, T_MERGE - 1)
            act.wait_ge(ml_ya, M_HEADS + 1)
            act.wait_ge(w_used, 2 * T_MERGE)
            for k in range(KT):
                nc.scalar.activation(XH[:, k, :], Y[:, k, :], ACT.Copy).then_inc(y_hi, 1)

            def sigmoids(i, u):
                act.wait_ge(sig_in[u], 32 * i + 32)
                nc.scalar.activation(GAB[:, u, :, :], GAB[:, u, :, :], ACT.Sigmoid).then_inc(sig_done, 1)

            with act.Fori(0, 8) as i:
                for u in range(2):
                    hi(i, 4, 2 * (T_MERGE + u) + 1)
                    sigmoids(i, u)
                    hi(i, 4, 2 * (T_MERGE + u) + 2)

            act.wait_ge(merged, 16 + 1)
            for k in range(KT):
                nc.scalar.activation(XH[:, k, :], Y[:, k, :], ACT.Copy).then_inc(m_hi, 1)
            act.wait_ge(m_lo, KT)

            def out_squares(n, nst):
                for b in range(5):
                    act.wait_ge(o_copied, 5 * n + (5 * nst + b + 1))
                    if nst or b or not isinstance(n, int):
                        act.wait_ge(o_sq, 5 * n + (5 * nst + b) + 1)
                    nc.scalar.activation(SQS, OR[:, b, bass.ds(512 * n + 512 * nst, 512)], ACT.Square,
                                         accum_out=SSQ[:, b, bass.ds(n + nst, 1)]).then_inc(o_sq, 1)

            for q in range(8):
                hi(0, 0, 2 * T_OUT + 1 + q)
            with act.Fori(0, 2) as n:
                for q in range(8):
                    hi(n, 8, 2 * T_OUT + 9 + q)
                    if q == 0:
                        out_squares(n, 0)
            for q in range(7):
                hi(0, 0, 2 * T_OUT + 25 + q)
                if q == 0:
                    out_squares(0, 2)
            out_squares(0, 3)

        @block.vector
        def _(dve):
            chain = Chain(dve, dve_chain)

            V = nc.vector

            def lo(i, per, gs):
                dve.wait_ge(hi_done, per * i + (gs + 1))
                V.tensor_tensor(WL[:, gs % 2, :], RAW[:, gs % 4, :], WH[:, gs % 2, :].bitcast(F32),
                                ALU.subtract).then_inc(lo_done, 1)

            dve.wait_ge(silu_e, 1)
            V.tensor_tensor(ROWS[0:32, :], ROWS[0:32, :], OUTS[0:32, 0, 0:P], ALU.mult).then_inc(silu_done, 1)
            dve.wait_ge(rows_t, 1)
            V.tensor_copy(VC[:, :], bank[7][:, 0:88]).then_inc(vc_done, 1)
            dve.wait_ge(sq_done, 5)
            V.tensor_scalar(SS[:, :], SS[:, :], 1.0 / D, EPS, ALU.mult, ALU.add).then_inc(ms_done, 1)
            dve.wait_ge(rstd_done, 1)
            for b in range(5):
                V.tensor_scalar(XT[:, b, :], XT[:, b, :], RSTD[:, b:b + 1], None, ALU.mult).then_inc(xn_done, 1)
            def mod_row(i, u):
                dve.wait_ge(ada_used, 16 * i + 8 * (u + 1))
                V.tensor_copy(MR[0:2, u, :], bank[4 + u][0:2, :]).then_inc(ada_row, 1)

            def mod_columns(i, c):
                dve.wait_ge(ada_t, 2 * i + (c + 1))
                V.tensor_copy(MODS[:, bass.ds(8 * i + 4 * c, 4), :],
                              bank[6 + c % 2][:, :].rearrange("p (n v) -> p n v", v=P)[:, :, 0:2]).then_inc(ada_out, 1)

            dve.wait_ge(mr_zero, 1)
            mod_row(0, 0)
            mod_row(0, 1)
            mod_columns(0, 0)
            with dve.Fori(1, 4) as i:
                for u in range(2):
                    mod_row(i, u)
                    mod_columns(i, u - 1)
            mod_columns(0, 7)
            dve.wait_ge(ada_out, 8)
            for v in range(2):
                ins = V.tensor_tensor(MODS[:, 0:32, v], MODS[:, 0:32, v], VC[:, 48:80], ALU.add)
            chain.link(ins)
            for v in range(2):
                ins = V.scalar_tensor_tensor(SCL[:, :, v], MODS[:, 16:32, v], 1.0, VC[:, 32:48], ALU.add, ALU.mult)
            ins.then_inc(scl_done, 1)
            for k in range(KT):
                dve.wait_ge(u_done, k + 1)
                V.tensor_copy(XH[:, k, :], OUTS[:, k % 2, :]).then_inc(u_hi, 1)
                dve.wait_ge(u_hi, k + 1)
                V.tensor_tensor(XL[:, k, :], OUTS[:, k % 2, :], XH[:, k, :].bitcast(F32), ALU.subtract).then_inc(u_lo, 1)
                if k == 9:
                    lo(0, 0, 0)

            lo(0, 0, 1)
            for t in range(1, T_L0):
                for x in range(2):
                    lo(0, 0, 2 * t + x)
                if t == 2:
                    R = slice(0, 36)
                    dve.wait_ge(scan_in, 16 * 10)
                    dve.wait_ge(pool_chain, 5)
                    chain.link(V.tensor_scalar(GI[R, :], GI[R, :], BIAS[R, 0:1], None, ALU.add))
                    chain.link(V.tensor_scalar(GT[R, :], GF[R, :], BIAS[R, 1:2], None, ALU.add))
                    V.scalar_tensor_tensor(GB[R, :], GT[R, :], -1.0, GT[R, :], ALU.mult, ALU.min).then_inc(scan_t, 1)
                    dve.wait_ge(scan_ln, 1)
                    chain.link(V.scalar_tensor_tensor(GT[R, :], GT[R, :], 0.0, GB[R, :], ALU.min, ALU.subtract))
                    for r in range(2):
                        at = slice(32 * r, 32 * r + 4)
                        for c0, c1 in ((0, LAT), (LAT, TOK)):
                            cs = slice(c0, c1) if r == 0 else slice(c1 - 1, c0 - 1 if c0 else None, -1)
                            first = M0R[at, :] if c0 == 0 else 0.0
                            V.tensor_tensor_scan(GB[at, cs], GT[at, cs], GT[at, cs], 0.0, ALU.add, ALU.bypass)
                            chain.link(V.tensor_tensor_scan(GM[at, cs], GT[at, cs], GI[at, cs], first, ALU.add, ALU.max))
                    for r in range(2):
                        at = slice(32 * r, 32 * r + 4)
                        V.tensor_tensor(TA[at, :], GI[at, :], GB[at, :], ALU.subtract)
                        V.tensor_scalar(TA[64 + 32 * r:68 + 32 * r, :], GM[at, :], -1.0, None, ALU.mult)
                        ins = V.tensor_tensor(GF[at, :], GB[at, :], GM[at, :], ALU.subtract)
                    ins.then_inc(scan_rows, 1)
                if t == 4:
                    dve.wait_ge(cols_psum, 1)
                    V.tensor_copy(COLS[:, :, :], ab[0][:, 0:500].rearrange("p (b c) -> p b c", b=5)).then_inc(cols_done, 1)
            dve.wait_ge(gacc_init, 32)
            with dve.Fori(0, 4) as ch:
                chain.enter(ch, PER_GATE)
                for q in range(8):
                    lo(ch, 8, 2 * T_L0 + q)
                    dve.wait_ge(gada_in[q % 2], 64 * ch + 16 * (q // 2 + 1))
                    for k in range(2):
                        for v in range(2):
                            acc = GACC[:, v, bass.ds(512 * ch, 512)]
                            at = 2 * q + k + 16 * v
                            ins = V.scalar_tensor_tensor(acc, AR[:, q % 2, 512 * k:512 * k + 512], VC[:, at:at + 1],
                                                         acc, ALU.mult, ALU.add)
                        if k == 0:
                            chain.link(ins)
                    ins.then_inc(gada_used, 1)
                    dve.wait_ge(gada_used, 8 * ch + (q + 1))
                chain.leave(4)

            dve.wait_ge(aconst_in, 16)
            with dve.Fori(0, KV_HEADS) as kv:
                chain.enter(kv, PER_KV)

                def prepare():
                    dve.wait_ge(prep_psum, kv + 1)
                    V.tensor_copy(VA[:, 0:5, :], ab[3][:, 0:320].rearrange("p (b d) -> p b d", b=5))
                    V.tensor_copy(KO, ab[3][:, 320:384])
                    V.tensor_copy(KK[:, 896:1024], ab[3][:, 384:512]).then_inc(kvo_ready, 1)
                    for j, x in enumerate((KK[:, P:P + LAT], QT[:, 0, 0:LAT], QT[:, 1, 0:LAT])):
                        V.tensor_tensor(RT, ab[j][:, :], sin, ALU.mult)
                        chain.link(V.tensor_tensor(x, x, cos, ALU.mult))
                        ins = V.tensor_tensor(x, x, RT, ALU.add)
                        if j < 2:
                            chain.link(ins)
                    ins.then_inc(roped, 1)

                def z_gate():
                    dve.wait_ge(ez_done, kv + 1)
                    chain.link(V.tensor_scalar(EZ, EZ, 1.0, None, ALU.add))
                    chain.link(V.reciprocal(EZ, EZ))
                    z = ZT.rearrange("p c t -> p (c t)")
                    chain.link(V.tensor_tensor(z, z, EZ, ALU.mult))

                def row_max(u):
                    par, pair, n = u % 2, u % 2, u // 2
                    dve.wait_ge(s_psum, 10 * kv + (u + 1))
                    if u >= 1:
                        dve.wait_ge(probs, 10 * kv + u)
                    if u >= 2:
                        dve.wait_ge(probs_t, 10 * kv + (u - 1))
                    V.tensor_copy(SE, SINK[:, 2 * pair:2 * pair + 2])
                    for e in range(2):
                        head = 2 * pair + e
                        if n < NB:
                            mask = band[0 if n == 0 else 2 if n == NB - 1 else 1]
                            ins = V.tensor_tensor_reduce(PR[:, par, e, :], ab[e][:, :], mask, SCALE,
                                                         SINK[:, head:head + 1], ALU.add, ALU.max, MXR[:, e:e + 1])
                        else:
                            ins = V.tensor_tensor_reduce(PR[:, par, e, 0:P], ab[e][:, 0:P], band[1][:, P:2 * P], SCALE,
                                                         SINK[:, head:head + 1], ALU.add, ALU.max, MXR[:, e:e + 1])
                    chain.link(ins)
                    V.tensor_tensor(SE, SE, MXR, ALU.subtract)
                    V.tensor_scalar(NM, MXR, -1.0, None, ALU.mult).then_inc(neg_max, 1)

                def denominators(u):
                    dve.wait_ge(probs, 10 * kv + (u + 1))
                    chain.link(V.tensor_tensor(RDEN, RSUM, SE, ALU.add))
                    chain.link(V.reciprocal(RDEN, RDEN))

                def normalise(u):
                    dve.wait_ge(o_psum, 10 * kv + (u + 1))
                    if u >= 1:
                        dve.wait_ge(ot_psum, 10 * kv + u)
                    for e in range(2):
                        ins = V.tensor_scalar(OB[:, HD * e:HD * e + HD], ab[2][:, HD * e:HD * e + HD],
                                              RDEN[:, e:e + 1], None, ALU.mult)
                    ins.then_inc(o_ready, 1)

                def gated(u):
                    n, pair = u // 2, u % 2
                    dve.wait_ge(ot_psum, 10 * kv + (u + 1))
                    V.tensor_tensor(Y[:, 2 * kv + (8 + pair), n * P:(n + 1) * P], ab[0][:, 0:P],
                                    ZT[:, pair, n * P:(n + 1) * P], ALU.mult).then_inc(yb_done, 1)

                for s in range(2 * L1_TILES):
                    lo(kv, 2 * L1_TILES, 2 * T_L1 + s)
                    if s == 1:
                        z_gate()
                    if s == 2:
                        prepare()
                    if s % 2 == 0 and s >= 6:
                        gated((s - 6) // 2)
                    if s % 2 == 1 and s >= 5:
                        normalise((s - 5) // 2)
                    if s % 2 == 1 and 3 <= s < 23:
                        row_max((s - 3) // 2)
                        denominators((s - 3) // 2)
                gated(9)
                chain.leave(KV_HEADS)

            dve.wait_ge(m0_in, 16)
            with dve.Fori(0, M_HEADS) as h:
                chain.enter(h, PER_HEAD)

                def small():
                    dve.wait_ge(ml_ya, h + 1)
                    for q in range(4):
                        V.tensor_copy(COLH[:, :, q:q + 1], COLS[:, :, bass.ds(h + 32 * q, 1)])
                    V.tensor_copy(M0H[:, :], M0B[:, :, h])
                    V.tensor_copy(MNH[:, :], VC[:, bass.ds(2 * h + 80, 2)])

                def token_major():
                    dve.wait_ge(ml_vt, h + 1)
                    for j in range(2):
                        V.tensor_copy(VT[:, 2 * j:2 * j + 2, 0:MD], ab[j][:, :].rearrange("p (b d) -> p b d", b=2))
                    V.tensor_copy(VT[:, 4, 0:MD], ab[2][:, 0:MD])
                    V.tensor_copy(KP, ab[2][:, MD:2 * MD]).then_inc(ml_vt_sb, 1)

                def masked():
                    for r in range(2):
                        for i in range(NB):
                            lo_ = p_at(r, i, i)
                            V.tensor_tensor(PM[r][:, lo_:lo_ + P], RB[:, r, i * P:(i + 1) * P], tri[r], ALU.add)
                        ins = V.tensor_tensor(PP[:, r, :], RB[:, r, LAT:TOK], tri[r], ALU.add)
                    ins.then_inc(ml_pre, 1)

                def weigh():
                    dve.wait_ge(ml_decay, h + 1)
                    dve.wait_ge(ml_s, h + 1)
                    for i in range(NB):
                        for r in range(2):
                            c0, c1 = (i * P, LAT) if r == 0 else (0, (i + 1) * P)
                            at = p_at(r, i, c0 // P)
                            pm = PM[r][:, at:at + c1 - c0]
                            ins = V.scalar_tensor_tensor(pm, ab[i][:, c0:c1], KSCALE, pm, ALU.mult, ALU.mult)
                    ins.then_inc(ml_p, 1)
                    for r in range(2):
                        ins = V.tensor_scalar(KW[:, r, :], KP, PP[:, r, (P - 1) * (1 - r):(P - 1) * (1 - r) + 1], KSCALE,
                                              ALU.mult, ALU.mult)
                    ins.then_inc(ml_kw, 1)

                def scaled_queries():
                    dve.wait_ge(ml_w, h + 1)
                    for r in range(2):
                        for cc in range(2):
                            ins = V.tensor_tensor(QS[r][:, cc, :], MQ[:, cc, 0:LAT], RB[:, r, 0:LAT], ALU.mult)
                    ins.then_inc(ml_qs, 1)

                def prompt_p():
                    dve.wait_ge(ml_sp, h + 1)
                    dve.wait_ge(ml_kw, h + 1)
                    for r in range(2):
                        ins = V.scalar_tensor_tensor(PP[:, r, :], ab[0][:, 0:P], KSCALE, PP[:, r, :], ALU.mult, ALU.mult)
                    ins.then_inc(ml_pp, 1)

                def quotient(bk, b, r):
                    chain.link(V.tensor_copy(DEN[:, 0:1], bk[:, MD:MD + 1]))
                    chain.link(V.scalar_tensor_tensor(DEN[:, 1:2], DEN[:, 0:1], -1.0, DEN[:, 0:1], ALU.mult, ALU.max))
                    chain.link(V.tensor_tensor(DEN[:, 1:2], DEN[:, 1:2], ENM[:, b, r:r + 1], ALU.max))
                    chain.link(V.reciprocal(DEN[:, 1:2], DEN[:, 1:2]))
                    if r == 0:
                        return V.tensor_scalar(HH[:, b, :], bk[:, 0:MD], DEN[:, 1:2], None, ALU.mult)
                    return V.scalar_tensor_tensor(HH[:, b, :], bk[:, 0:MD], DEN[:, 1:2], HH[:, b, :], ALU.mult, ALU.add)

                def statistics():
                    dve.wait_ge(ml_ubd, h + 1)
                    for b in range(5):
                        ins = V.bn_stats(BNS[:, b, :], HH[:, b, :])
                    chain.link(ins)
                    for cc in range(2):
                        ins = V.tensor_copy(CA[:, 1, cc, :], ab[2 + cc][:, 0:257])
                    ins.then_inc(ml_cbd, 1)
                    for b in range(5):
                        ins = V.bn_aggr(MVAR[:, b, :], BNS[:, b, :])
                    chain.link(ins)
                    V.tensor_scalar(MVAR[:, :, 1], MVAR[:, :, 1], EPS, None, ALU.add).then_inc(ml_var, 1)

                for s in range(2 * L2_TILES):
                    lo(h, 2 * L2_TILES, 2 * T_L2 + s)
                    if s == 0:
                        small()
                    if s == 1:
                        dve.wait_ge(ml_in, 16 * 11 * h + 16 * 11)
                        token_major()
                    if s == 2:
                        dve.wait_ge(ml_vt, h + 1)
                        masked()
                    if s == 3:
                        weigh()
                    if s == 4:
                        dve.wait_ge(ml_s, h + 1)
                        prompt_p()
                        scaled_queries()
                    if s == 5:
                        dve.wait_ge(ml_uf, h + 1)
                        for b in range(NB):
                            ins = quotient(ab[b], b, 0)
                        ins.then_inc(ml_ufd, 1)
                    if s == 6:
                        dve.wait_ge(ml_ub, h + 1)
                        dve.wait_ge(ml_ufd, h + 1)
                        for b in range(NB):
                            ins = quotient(ab[b], b, 1)
                        ins.then_inc(ml_ubd, 1)
                    if s == 7:
                        dve.wait_ge(ml_up, h + 1)
                        chain.link(quotient(ab[0], NB, 0))
                        chain.link(quotient(ab[1], NB, 1))
                        for cc in range(2):
                            ins = V.tensor_copy(CA[:, 0, cc, :], ab[2 + cc][:, 0:257])
                        ins.then_inc(ml_upd, 1)
                    if s == 8:
                        dve.wait_ge(ml_cb, h + 1)
                        statistics()
                    if s == 9:
                        dve.wait_ge(ml_rs, h + 1)
                        for b in range(5):
                            ins = V.tensor_scalar(HH[:, b, :], HH[:, b, :], MVAR[:, b, 0:1], MRS[:, b:b + 1],
                                                  ALU.subtract, ALU.mult)
                        ins.then_inc(ml_h, 1)
                    if s == 10:
                        dve.wait_ge(ml_eg, h + 1)
                        eo = MK.rearrange("p c t -> p (c t)")
                        ez = MQ.rearrange("p c t -> p (c t)")
                        z = MVT.rearrange("p c t -> p (c t)")
                        chain.link(V.tensor_scalar(ez, ez, 1.0, None, ALU.add))
                        chain.link(V.scalar_tensor_tensor(ez, eo, 1.0, ez, ALU.add, ALU.mult))
                        chain.link(V.reciprocal(ez, ez))
                        chain.link(V.tensor_tensor(z, z, ez, ALU.mult))
                    if s == 11:
                        dve.wait_ge(ml_ht, h + 1)
                        for cc in range(2):
                            V.scalar_tensor_tensor(Y[:, 2 * h + cc, 0:LAT], ab[cc][:, :], MNH[:, cc:cc + 1],
                                                   MVT[:, cc, 0:LAT], ALU.mult, ALU.mult)
                            ins = V.scalar_tensor_tensor(Y[:, 2 * h + cc, LAT:TOK], ab[2][:, cc * P:(cc + 1) * P],
                                                         MNH[:, cc:cc + 1], MVT[:, cc, LAT:TOK], ALU.mult, ALU.mult)
                        ins.then_inc(ml_ya, 1)
                chain.leave(M_HEADS)

            lo(0, 0, 2 * T_MERGE)
            for k in range(KT):
                dve.wait_ge(y_hi, k + 1)
                V.tensor_tensor(XL[:, k, :], Y[:, k, :], XH[:, k, :].bitcast(F32), ALU.subtract).then_inc(y_lo, 1)

            def merge(i, u):
                dve.wait_ge(merged, 2 * i + u + 1)
                dve.wait_ge(w_used, 4 * i + (2 * (T_MERGE + u) + 2))
                dve.wait_ge(sig_done, 2 * i + (u + 1))
                for gi in range(2):
                    for n in range(2):
                        cs = slice(n * HALF_TOK, (n + 1) * HALF_TOK)
                        ins = V.tensor_tensor(MT[:, gi, cs], bank[4 * u + 2 * gi + n][:, 0:HALF_TOK],
                                              GAB[:, u, gi, cs], ALU.mult)
                chain.link(ins)
                V.tensor_tensor(Y[:, 2 * i + u, :], MT[:, 0, :], MT[:, 1, :], ALU.add).then_inc(merged, 1)

            with dve.Fori(0, 8) as i:
                chain.enter(i, 2)
                for u in range(2):
                    lo(i, 4, 2 * (T_MERGE + u) + 1)
                    lo(i, 4, 2 * (T_MERGE + u) + 2)
                    merge(i, u)
                chain.leave(8)

            for k in range(KT):
                dve.wait_ge(m_hi, k + 1)
                V.tensor_tensor(XL[:, k, :], Y[:, k, :], XH[:, k, :].bitcast(F32), ALU.subtract).then_inc(m_lo, 1)
            dve.wait_ge(m_lo, KT)

            def out_copy(n, nst):
                dve.wait_ge(w_used, 8 * n + (2 * T_OUT + 8 * nst + 8))
                for b in range(5):
                    V.tensor_copy(OR[:, b, bass.ds(512 * n + 512 * nst, 512)], bank[b][:, :]).then_inc(o_copied, 1)

            def gate_rows(j):
                dve.wait_ge(gw_psum, j + 1)
                cs = slice(512 * (j % 4), 512 * (j % 4) + 512)
                V.tensor_tensor(GW[:, j // 4, cs], bank[5 + j % 2][:, :], NPW[:, cs], ALU.mult).then_inc(gw_done, 1)

            dve.wait_ge(gs_in, 32)
            for q in range(8):
                lo(0, 0, 2 * T_OUT + 1 + q)
                gate_rows(q)
            with dve.Fori(0, 2) as n:
                out_copy(n, 0)
                for q in range(8):
                    lo(n, 8, 2 * T_OUT + 9 + q)
            out_copy(0, 2)
            for q in range(7):
                lo(0, 0, 2 * T_OUT + 25 + q)
            out_copy(0, 3)
            dve.wait_ge(o_sq, 20 + 1)
            chain.link(V.tensor_reduce(SS[:, :], SSQ, AX_X, ALU.add))
            V.tensor_scalar(SS[:, :], SS[:, :], 1.0 / D, EPS, ALU.mult, ALU.add).then_inc(o_ms, 1)
            dve.wait_ge(o_root, 1)
            dve.wait_ge(gw_done, 8)
            for b in range(5):
                chain.link(V.scalar_tensor_tensor(OR[:, b, :], OR[:, b, :], RSTD[:, b:b + 1], GW[:, b // NB, :],
                                                  ALU.mult, ALU.mult))
                dve.wait_ge(xr_in[b % 3], 16 * (b // 3 + 1))
                V.tensor_tensor(OR[:, b, :], XR[:, b % 3, :], OR[:, b, :], ALU.add).then_inc(o_y, 1)

        @block.tensor
        def _(pe):
            def transpose(out, in_, k=P):
                return pe.transpose(out, in_, ident[0:k, 0:k])

            pe.wait_ge(const_in, 16)
            pe.wait_ge(rows_in, 16 * 5)
            pe.wait_ge(silu_done, 1)
            transpose(bank[7][:, 0:88], ROWS[:, :], 88).then_inc(rows_t, 1)
            pe.wait_ge(vc_done, 1)

            def mod_columns(i, c, first):
                pe.wait_ge(ada_row, 2 * i + (c + 1))
                if not first:
                    pe.wait_ge(ada_out, 2 * i + (c - 1))
                for n in range(4):
                    ins = transpose(bank[6 + c % 2][:, n * P:(n + 1) * P], MR[:, c % 2, n * P:(n + 1) * P])
                ins.then_inc(ada_t, 1)

            def mod_chunk(i, u, first):
                if not first:
                    pe.wait_ge(ada_row, 2 * i + (u - 1))
                for q in range(8):
                    pe.wait_ge(raw_in[q % 4], 64 * i + 16 * (2 * u + q // 4 + 1))
                    wv = RAW[:, q % 4, :].rearrange("p (k n) -> p k n", k=2)
                    for k in range(2):
                        kt = 2 * q + k
                        ins = pe.matmul(bank[4 + u][0:2, :], VC[:, kt:kt + 17:16], wv[:, k, :],
                                        start=(kt == 0), stop=(kt == KT - 1))
                    ins.then_inc(ada_used, 1)
                    if q == 1 and not (first and u == 0):
                        mod_columns(i, u - 1, first)

            for u in range(2):
                mod_chunk(0, u, True)
            with pe.Fori(1, 4) as i:
                for u in range(2):
                    mod_chunk(i, u, False)
            mod_columns(0, 7, False)

            pe.wait_ge(xn_done, 5)
            for k in range(KT):
                if k >= 2:
                    pe.wait_ge(u_done, k - 1)
                for b in range(5):
                    out = bank[2 * (k % 2)][:, b * P:(b + 1) * P] if b < NB else bank[2 * (k % 2) + 1][:, 0:P]
                    ins = transpose(out, XT[:, b, k * P:(k + 1) * P])
                ins.then_inc(xt_psum, 1)
            pe.wait_ge(u_done, KT)

            def product(banks, wslot, k0, kk, first, last, k_wait=None):
                wh = WH[:, wslot, :].rearrange("p (k n) -> p k n", k=8)
                wl = WL[:, wslot, :].rearrange("p (k n) -> p k n", k=8)
                for k in range(8):
                    if k_wait is not None:
                        pe.wait_ge(k_wait, k0 + k + 1)
                    for wi, (w, x) in enumerate(((wh, XH), (wh, XL), (wl, XH))):
                        for n in range(2):
                            ins = pe.matmul(banks[n][:, 0:HALF_TOK], w[:, k, :],
                                            x[:, k0 + k, n * HALF_TOK:(n + 1) * HALF_TOK],
                                            start=(first and k == 0 and wi == 0), stop=(last and k == 7 and wi == 2))
                return ins

            def half(i2, i, t, x, k_wait=None):
                if x == 0 and not (isinstance(i, int) and t + i < 2):
                    pe.wait_ge(out_ready, i + (t - 1))
                pe.wait_ge(lo_done, i2 + (2 * t + x + 1))
                ins = product(bank[2 * (t % 2):2 * (t % 2) + 2], x, 8 * x, 8, x == 0, x == 1, k_wait)
                ins.then_inc(w_used, 1)

            for x in range(2):
                half(0, 0, 0, x, u_lo)
            for t in range(1, T_L0):
                for x in range(2):
                    if t == 4 and x == 0:
                        pe.wait_ge(scan_rows, 1)
                        for b in range(5):
                            ins = transpose(ab[0][:, 100 * b:100 * b + 100], TA[0:100, b * P:(b + 1) * P], 100)
                        ins.then_inc(cols_psum, 1)
                    half(0, 0, t, x)
            pe.wait_ge(cols_done, 1)

            with pe.Fori(0, 4) as ch:
                for k in range(4):
                    for x in range(2):
                        half(8 * ch, 4 * ch, T_L0 + k, x)
            pe.wait_ge(aconst_in, 16)
            pe.wait_ge(pads_zero, 1)

            with pe.Fori(0, KV_HEADS) as kv:
                def prepare():
                    pe.wait_ge(att_in, 11 * 16 * kv + 11 * 16)
                    pe.wait_ge(yb_done, 10 * kv + 1)
                    for j, x in enumerate((KK[:, P:P + LAT], QT[:, 0, 0:LAT], QT[:, 1, 0:LAT])):
                        pe.matmul(ab[j][:, :], perm, x, start=True, stop=True)
                    for b in range(5):
                        transpose(ab[3][:, HD * b:HD * b + HD], VVT[0:HD, b * P:(b + 1) * P], HD)
                    transpose(ab[3][:, 320:384], KK[0:HD, 768:896], HD)
                    transpose(ab[3][:, 384:512], CKG).then_inc(prep_psum, 1)

                def scores(u):
                    n, pair = u // 2, u % 2
                    if u == 0:
                        pe.wait_ge(roped, kv + 1)
                    if u >= 2:
                        pe.wait_ge(yb_done, 10 * kv + u)
                    if u >= 1:
                        pe.wait_ge(neg_max, 10 * kv + u)
                    for e in range(2):
                        at = slice(HD * e, HD * e + HD)
                        q = QT[at, pair, n * P:(n + 1) * P]
                        if n < NB:
                            pe.matmul(ab[e][:, 0:384], q, KK[at, n * P:n * P + 384], start=True, stop=True)
                            ins = pe.matmul(ab[e][:, 384:512], q, KK[at, 896:1024], start=True, stop=True)
                        else:
                            ins = pe.matmul(ab[e][:, 0:P], q, KK[at, 768:896], start=True, stop=True)
                    ins.then_inc(s_psum, 1)

                def key_blocks(u):
                    n = u // 2
                    if n == NB:
                        return [(0, NB)]
                    return [(j, n - 1 + j) for j in range(3) if 0 <= n - 1 + j < NB] + [(3, 5)]

                def probs_transposed(u):
                    pe.wait_ge(probs, 10 * kv + (u + 1))
                    if u >= 1:
                        pe.wait_ge(o_ready, 10 * kv + u)
                    for e in range(2):
                        for j, _ in key_blocks(u):
                            ins = transpose(ab[2 + e][:, j * P:(j + 1) * P], PR[:, u % 2, e, j * P:(j + 1) * P])
                    ins.then_inc(probs_t, 1)

                def attend(u):
                    pe.wait_ge(probs_t_sb, 10 * kv + (u + 1))
                    blocks = key_blocks(u)
                    for e in range(2):
                        for m, (j, vb) in enumerate(blocks):
                            ins = pe.matmul(ab[2][:, HD * e:HD * e + HD], PT[:, e, j * P:(j + 1) * P], VA[:, vb, :],
                                            start=(m == 0), stop=(m == len(blocks) - 1))
                    ins.then_inc(o_psum, 1)

                def out_transposed(u):
                    pe.wait_ge(o_ready, 10 * kv + (u + 1))
                    if u < 9:
                        pe.wait_ge(neg_max, 10 * kv + (u + 2))
                    transpose(ab[0][:, 0:P], OB).then_inc(ot_psum, 1)

                for s in range(2 * L1_TILES):
                    if s == 2:
                        prepare()
                    if s % 2 == 0 and s >= 6:
                        out_transposed((s - 6) // 2)
                    if s % 2 == 1 and s >= 5:
                        attend((s - 5) // 2)
                    if s % 2 == 1 and 3 <= s < 23:
                        scores((s - 3) // 2)
                    if s % 2 == 0 and s >= 4:
                        probs_transposed((s - 4) // 2)
                    t, x = divmod(s, 2)
                    half(2 * L1_TILES * kv, L1_TILES * kv, T_L1 + t, x)
                out_transposed(9)

            pe.wait_ge(ones_col, 1)
            with pe.Fori(0, M_HEADS) as h:
                def token_major():
                    pe.wait_ge(ml_in, 16 * 11 * h + 16 * 11)
                    pe.wait_ge(yb_done, 10 * KV_HEADS + 1)
                    pe.wait_ge(ml_ya, h + 1)
                    for b in range(5):
                        for cc in range(2):
                            transpose(ab[b // 2][:, MD * (b % 2) + P * cc:MD * (b % 2) + P * (cc + 1)],
                                      MVT[:, cc, b * P:(b + 1) * P])
                    for cc in range(2):
                        ins = transpose(ab[2][:, MD + P * cc:MD + P * (cc + 1)], MK[:, cc, LAT:TOK])
                    ins.then_inc(ml_vt, 1)

                def key_query(bk, kcols, qcols, n):
                    for cc in range(2):
                        ins = pe.matmul(bk[:, 0:n], MK[:, cc, kcols], MQ[:, cc, qcols], start=(cc == 0), stop=(cc == 1))
                    return ins

                def read_out(r):
                    for t in range(NB):
                        srcs = range(t + 1) if r == 0 else range(t, NB)
                        for m, i in enumerate(srcs):
                            at = p_at(r, i, t)
                            pe.matmul(ab[t][:, 0:257], PM[r][:, at:at + P], VT[:, i, :], start=(m == 0), stop=False)
                        for cc in range(2):
                            ins = pe.matmul(ab[t][:, 0:257], QS[r][:, cc, t * P:(t + 1) * P], CA[:, r, cc, :],
                                            start=False, stop=(cc == 1))
                    return ins

                def state(r):
                    for cc in range(2):
                        ins = pe.matmul(ab[2 + cc][:, 0:257], KW[:, r, cc * P:(cc + 1) * P], VT[:, NB, :],
                                        start=True, stop=True)
                    return ins

                for s in range(2 * L2_TILES):
                    if s == 1:
                        token_major()
                    if s == 2:
                        pe.wait_ge(ml_vt_sb, h + 1)
                        for i in range(NB):
                            ins = key_query(ab[i], slice(i * P, (i + 1) * P), slice(0, LAT), LAT)
                        ins.then_inc(ml_s, 1)
                    if s == 4:
                        pe.wait_ge(ml_p, h + 1)
                        key_query(ab[0], slice(LAT, TOK), slice(LAT, TOK), P).then_inc(ml_sp, 1)
                    if s == 5:
                        pe.wait_ge(ml_qs, h + 1)
                        pe.wait_ge(ml_pp, h + 1)
                        read_out(0).then_inc(ml_uf, 1)
                    if s == 6:
                        pe.wait_ge(ml_ufd, h + 1)
                        read_out(1).then_inc(ml_ub, 1)
                    if s == 7:
                        pe.wait_ge(ml_ubd, h + 1)
                        for r in range(2):
                            pe.matmul(ab[r][:, 0:257], PP[:, r, :], VT[:, NB, :], start=True, stop=True)
                        state(0).then_inc(ml_up, 1)
                    if s == 8:
                        pe.wait_ge(ml_upd, h + 1)
                        state(1).then_inc(ml_cb, 1)
                    if s == 10:
                        pe.wait_ge(ml_h, h + 1)
                        for cc in range(2):
                            for b in range(5):
                                out = ab[cc][:, b * P:(b + 1) * P] if b < NB else ab[2][:, cc * P:(cc + 1) * P]
                                ins = transpose(out, HH[:, b, cc * P:(cc + 1) * P])
                        ins.then_inc(ml_ht, 1)
                    t, x = divmod(s, 2)
                    half(2 * L2_TILES * h, L2_TILES * h, T_L2 + t, x)

            pe.wait_ge(out_ready, T_MERGE)
            pe.wait_ge(ml_ya, M_HEADS + 1)

            def merge_tile(i, u, k_wait):
                if k_wait is None:
                    pe.wait_ge(merged, 2 * i + u)
                for x in range(2):
                    pe.wait_ge(lo_done, 4 * i + (2 * (T_MERGE + u) + x + 1))
                    b0 = 4 * u + 2 * x
                    product(bank[b0:b0 + 2], x, 8 * x, 8, True, True, k_wait).then_inc(w_used, 1)

            for u in range(2):
                merge_tile(0, u, y_lo)
            with pe.Fori(1, 8) as i:
                for u in range(2):
                    merge_tile(i, u, None)

            pe.wait_ge(merged, 16 + 1)
            pe.wait_ge(ones_set, 1)
            pe.wait_ge(gs_in, 32)

            def out_half(i8, q, k_wait, copied):
                pe.wait_ge(lo_done, i8 + (2 * T_OUT + q + 1))
                wh = WH[:, q % 2, :].rearrange("p (k n) -> p k n", k=2)
                wl = WL[:, q % 2, :].rearrange("p (k n) -> p k n", k=2)
                for k in range(2):
                    kt = 2 * q + k
                    if k_wait:
                        pe.wait_ge(m_lo, kt + 1)
                    for b in range(5):
                        if kt == 0 and copied is not None:
                            pe.wait_ge(o_copied, copied + b)
                        toks = slice(b * P, (b + 1) * P)
                        for wi, (x, w) in enumerate(((XH, wh), (XH, wl), (XL, wh))):
                            ins = pe.matmul(bank[b][:, :], x[:, kt, toks], w[:, k, :],
                                            start=(kt == 0 and wi == 0), stop=(kt == KT - 1 and wi == 2))
                ins.then_inc(w_used, 1)

            for q in range(8):
                out_half(0, q, True, None)
                if q >= 2:
                    pe.wait_ge(gw_done, q - 1)
                pe.matmul(bank[5 + q % 2][:, :], ONES[:, :], GS[:, q // 4, 512 * (q % 4):512 * (q % 4) + 512],
                          start=True, stop=True).then_inc(gw_psum, 1)
            with pe.Fori(0, 3) as n:
                for q in range(8):
                    out_half(8 * n + 8, q, False, 5 * n + 1)


PER_GATE = 8
PER_KV = 3 + 5 + 10 * 3
PER_HEAD = 10 * 4 + 2 + 2 + 3 + 1


def p_at(r, i, t):
    if r == 0:
        return P * (i * 4 - i * (i - 1) // 2 + (t - i))
    return P * (i * (i + 1) // 2 + t)


_INS = ['x_prompt', 'x_sample', 'cache_k', 'cache_v', 'state_C', 'state_n', 'state_m', 'c', 'c_ctx', 'w_ada', 'b_ada',
        'norm_pre_w', 'norm_post_w', 'w_in', 'b_gates', 'mlstm_norm_w', 'attn_sink', 'w_proj_a', 'w_proj_b', 'w_out']
_OUTS = [(1, 128, 2048), (1, 512, 2048), (1, 1, 128, 4, 64), (1, 1, 128, 4, 64), (1, 1, 2, 4, 256, 256),
         (1, 1, 2, 4, 256), (1, 1, 2, 4)]


def kernel(**inputs):
    import concourse.bacc as _bacc
    from concourse.bass_utils import run_bass_kernel_spmd as _run

    nc = _bacc.Bacc("TRN2", target_bir_lowering=False, num_devices=1)
    arrays, args = {}, []
    for name in _INS:
        a = np.ascontiguousarray(inputs[name])
        arrays[f"in_{name}_dram"] = a
        args.append(nc.dram_tensor(f"in_{name}_dram", a.shape, mybir.dt.from_np(a.dtype), kind="ExternalInput").ap())
    arrays["constants_dram"] = shape_constants()
    args.append(nc.dram_tensor("constants_dram", (P, C_END), F32, kind="ExternalInput").ap())
    for i, shape in enumerate(_OUTS):
        args.append(nc.dram_tensor(f"out_{i}_dram", shape, F32, kind="ExternalOutput").ap())
    hybrid_layer(nc, *args)
    r = _run(nc, [arrays], core_ids=[0])
    return tuple(r.results[0][f"out_{i}_dram"] for i in range(len(_OUTS)))
```
